# Optimizing a Trainium2 kernel written in Bass

```python
import jax, jax.numpy as jnp
from jax import lax
import numpy as np

D_MODEL = 1024
BATCH = 1
SEQ = 256
DEPTH = 2

N_MIXERS = 2
N_HEADS = 16
HEAD_DIM = D_MODEL // N_HEADS
MOBA_BLOCK = 256
MOBA_TOPK = 3
Q_CHUNK = 128
POOL_WINDOWS = (2, 4, 8, 16)
N_POOL_GROUPS = len(POOL_WINDOWS)
POOL_GROUP_DIM = D_MODEL // N_POOL_GROUPS
D_FF = ((8 * D_MODEL // 3 + 127) // 128) * 128
N_ATTN_LAYERS = (DEPTH + N_MIXERS - 1) // N_MIXERS
N_POOL_LAYERS = DEPTH // N_MIXERS
EPS = 1e-6
NEG = -1e30

kernel_name = "hybrid_moba_pool_macaron"

def rmsnorm(x, g):
    xf = x.astype(jnp.float32)
    y = xf * lax.rsqrt(jnp.mean(xf * xf, axis=-1, keepdims=True) + EPS)
    return (y * g.astype(jnp.float32)).astype(x.dtype)

def swiglu(h, w_gate, w_up, w_down):
    return (jax.nn.silu(h @ w_gate) * (h @ w_up)) @ w_down

def alibi_slopes(n_heads):
    return jnp.exp2(-8.0 * jnp.arange(1, n_heads + 1, dtype=jnp.float32) / n_heads)

def moba_attention(h, w_qkv, w_o):
    B, S, D = h.shape
    H, dh, BS = N_HEADS, HEAD_DIM, MOBA_BLOCK
    qkv = h @ w_qkv
    q, k, v = jnp.split(qkv, 3, axis=-1)
    q = q.reshape(B, S, H, dh).astype(jnp.float32) * (dh ** -0.5)
    k = k.reshape(B, S, H, dh).astype(jnp.float32)
    v = v.reshape(B, S, H, dh).astype(jnp.float32)
    nb = -(-S // BS)
    pad = nb * BS - S
    k_pad = jnp.pad(k, ((0, 0), (0, pad), (0, 0), (0, 0)))
    v_pad = jnp.pad(v, ((0, 0), (0, pad), (0, 0), (0, 0)))
    k_blk = k_pad.reshape(B, nb, BS, H, dh).transpose(0, 3, 1, 2, 4)
    v_blk = v_pad.reshape(B, nb, BS, H, dh).transpose(0, 3, 1, 2, 4)
    k_mean = jnp.mean(k_blk, axis=3)
    slopes = alibi_slopes(H)
    n_sel = min(MOBA_TOPK, nb)
    b_ix = jnp.arange(B)[:, None, None, None]
    h_ix = jnp.arange(H)[None, None, :, None]

    def chunk(ci):
        t0 = ci * Q_CHUNK
        qc = lax.dynamic_slice_in_dim(q, t0, Q_CHUNK, axis=1)
        tpos = t0 + jnp.arange(Q_CHUNK, dtype=jnp.int32)
        j = t0 // BS
        gate = jnp.einsum('bchd,bhnd->bchn', qc, k_mean)
        gate = jnp.where(jnp.arange(nb) < j, gate, NEG)
        _, sel = lax.top_k(gate, n_sel)
        valid = jnp.arange(n_sel) < j
        kg = k_blk[b_ix, h_ix, sel]
        vg = v_blk[b_ix, h_ix, sel]
        kpos_sel = sel[..., None] * BS + jnp.arange(BS, dtype=jnp.int32)
        dist_sel = (tpos[None, :, None, None, None] - kpos_sel).astype(jnp.float32)
        s_sel = jnp.einsum('bchd,bchksd->bchks', qc, kg)
        s_sel = s_sel - slopes[None, None, :, None, None] * dist_sel
        s_sel = jnp.where(valid[None, None, None, :, None], s_sel, NEG)
        k_own = lax.dynamic_slice_in_dim(k_pad, j * BS, BS, axis=1)
        v_own = lax.dynamic_slice_in_dim(v_pad, j * BS, BS, axis=1)
        kpos_own = j * BS + jnp.arange(BS, dtype=jnp.int32)
        dist_own = tpos[:, None] - kpos_own[None, :]
        s_own = jnp.einsum('bchd,bshd->bchs', qc, k_own)
        s_own = s_own - slopes[None, None, :, None] * dist_own.astype(jnp.float32)[None, :, None, :]
        s_own = jnp.where((dist_own >= 0)[None, :, None, :], s_own, NEG)
        scores = jnp.concatenate([s_sel.reshape(B, Q_CHUNK, H, n_sel * BS), s_own], axis=-1)
        p = jax.nn.softmax(scores, axis=-1)
        p_sel = p[..., :n_sel * BS].reshape(B, Q_CHUNK, H, n_sel, BS)
        o = (jnp.einsum('bchks,bchksd->bchd', p_sel, vg)
             + jnp.einsum('bchs,bshd->bchd', p[..., n_sel * BS:], v_own))
        return o

    outs = lax.map(chunk, jnp.arange(S // Q_CHUNK, dtype=jnp.int32))
    o = outs.transpose(1, 0, 2, 3, 4).reshape(B, S, D).astype(h.dtype)
    return o @ w_o

def pool_mixer(h, w_pool, scale):
    B, S, D = h.shape
    G = POOL_GROUP_DIM
    hf = h.astype(jnp.float32)
    csum = jnp.concatenate([jnp.zeros((B, 1, D), jnp.float32), lax.cumsum(hf, axis=1)], axis=1)
    t = jnp.arange(S, dtype=jnp.int32)
    groups = []
    for g, w in enumerate(POOL_WINDOWS):
        c = csum[:, :, g * G:(g + 1) * G]
        lo = jnp.maximum(t + 1 - w, 0)
        win_sum = c[:, 1:] - c[:, lo]
        cnt = jnp.minimum(t + 1, w).astype(jnp.float32)
        groups.append(win_sum / cnt[None, :, None] - hf[:, :, g * G:(g + 1) * G])
    y = jnp.stack(groups, axis=2).astype(h.dtype)
    y = jnp.einsum('bsgc,gce->bsge', y, w_pool).reshape(B, S, D)
    return y * scale

def setup_inputs(seed: int = 0) -> dict:
    key = jax.random.key(seed)
    ks = jax.random.split(key, 11)
    f32 = jnp.float32
    x = jax.random.normal(ks[0], (BATCH, SEQ, D_MODEL), f32)
    ln_gains = 1.0 + 0.02 * jax.random.normal(ks[1], (DEPTH, 3, D_MODEL), f32)
    ffn_w_gate = jax.random.normal(ks[2], (DEPTH, 2, D_MODEL, D_FF), f32) * D_MODEL ** -0.5
    ffn_w_up = jax.random.normal(ks[3], (DEPTH, 2, D_MODEL, D_FF), f32) * D_MODEL ** -0.5
    ffn_w_down = jax.random.normal(ks[4], (DEPTH, 2, D_FF, D_MODEL), f32) * D_FF ** -0.5
    attn_w_qkv = jax.random.normal(ks[5], (N_ATTN_LAYERS, D_MODEL, 3 * D_MODEL), f32) * D_MODEL ** -0.5
    attn_w_o = jax.random.normal(ks[6], (N_ATTN_LAYERS, D_MODEL, D_MODEL), f32) * D_MODEL ** -0.5
    pool_w = jax.random.normal(ks[7], (N_POOL_LAYERS, N_POOL_GROUPS, POOL_GROUP_DIM, POOL_GROUP_DIM), f32) * POOL_GROUP_DIM ** -0.5
    pool_scale = 1.0 + 0.1 * jax.random.normal(ks[8], (N_POOL_LAYERS, D_MODEL), f32)
    final_gain = 1.0 + 0.02 * jax.random.normal(ks[9], (D_MODEL,), f32)
    return {"x": x, "ln_gains": ln_gains, "ffn_w_gate": ffn_w_gate, "ffn_w_up": ffn_w_up,
            "ffn_w_down": ffn_w_down, "attn_w_qkv": attn_w_qkv, "attn_w_o": attn_w_o,
            "pool_w": pool_w, "pool_scale": pool_scale, "final_gain": final_gain}

def reference(x, ln_gains, ffn_w_gate, ffn_w_up, ffn_w_down, attn_w_qkv, attn_w_o, pool_w, pool_scale, final_gain):
    for i in range(DEPTH):
        h = rmsnorm(x, ln_gains[i, 0])
        x = x + 0.5 * swiglu(h, ffn_w_gate[i, 0], ffn_w_up[i, 0], ffn_w_down[i, 0])
        h = rmsnorm(x, ln_gains[i, 1])
        m = i // N_MIXERS
        if i % N_MIXERS == 0:
            x = x + moba_attention(h, attn_w_qkv[m], attn_w_o[m])
        else:
            x = x + pool_mixer(h, pool_w[m], pool_scale[m])
        h = rmsnorm(x, ln_gains[i, 2])
        x = x + 0.5 * swiglu(h, ffn_w_gate[i, 1], ffn_w_up[i, 1], ffn_w_down[i, 1])
    return rmsnorm(x, final_gain)


_drawn_inputs = setup_inputs


def setup_inputs(seed=0):
    import zlib

    import numpy as np

    out = dict(_drawn_inputs(seed))
    spreads = {}
    factors = {}
    for name, (base, spread) in spreads.items():
        noise = np.random.default_rng([zlib.crc32(name.encode()), seed]).standard_normal(out[name].shape)
        drawn = base * np.exp(spread * noise) if base else spread * noise
        out[name] = __import__('jax').numpy.asarray(drawn.astype(out[name].dtype))
    for name, factor in factors.items():
        out[name] = (out[name] * factor).astype(out[name].dtype)
    return out
```

```python
from contextlib import ExitStack

import concourse.bass as bass
from concourse import mybir


def build_trunk(nc, x_in, ln_gains, w_gate, w_up, w_down, w_qkv, w_o, pool_w, pool_scale, final_gain, out):
    f32 = mybir.dt.float32
    f32r = mybir.dt.float32r
    ALU = mybir.AluOpType
    ACT = mybir.ActivationFunctionType
    AX = mybir.AxisListType

    P = 128
    SEQ, D = x_in.shape[1], x_in.shape[2]
    F = w_gate.shape[3]
    DC = D // P
    TT = SEQ // P
    DB = DC // 2
    GW = 256
    GM = GW // P
    GROUPS = F // GW
    HD = 64
    HEADS = D // HD
    QH = GW // HD
    QUADS = HEADS // QH
    WINDOWS = (2, 4, 8, 16)
    NPG = len(WINDOWS)
    EPS = 1e-6
    NEG = -1e30
    ROWS = DC * GW
    RAW = 3
    SPL = 6
    BODY = 6
    assert GROUPS % 2 == 1 and F % GW == 0 and SEQ == 2 * P and GM * D == ROWS and SPL == BODY and BODY % RAW == 0
    PAIRS = (GROUPS - 1) // 2
    FFN_TILES = 3 * GROUPS
    ATT_TILES = 4 * QUADS

    COUNTS = 3 + 2 * NPG
    CONSTS = COUNTS + 5 + NPG * 3 * TT

    FFN0, ATT0, FFN1 = 0, FFN_TILES, FFN_TILES + ATT_TILES
    FFN2 = FFN1 + FFN_TILES
    POOL0 = FFN2 + FFN_TILES
    FFN3 = POOL0 + 1
    TILES = FFN3 + FFN_TILES

    ctx = ExitStack()
    with ctx:
        def sb(name, shape, dt=f32):
            return ctx.enter_context(nc.sbuf_tensor(name, shape, dt))

        def sem(name):
            return ctx.enter_context(nc.semaphore(name))

        raw = sb("raw", [P, RAW, ROWS])
        w_hi = sb("w_hi", [P, SPL, ROWS], f32r)
        w_lo = sb("w_lo", [P, SPL, ROWS], f32r)
        x = sb("x", [P, DC, SEQ])
        xg_hi = sb("xg_hi", [P, DC, SEQ], f32r)
        xg_lo = sb("xg_lo", [P, DC, SEQ], f32r)
        gains_rows = sb("gains_rows", [64, P])
        gains = sb("gains", [P, 64])
        ident = sb("ident", [P, P])
        ones = sb("ones", [P, P])
        sq_sum = sb("sq_sum", [P, SEQ])
        mean = sb("mean", [P, SEQ + TT])
        rms_sq = sb("rms_sq", [P, SEQ + TT])
        rstd = sb("rstd", [P, SEQ + TT])
        rstd_t = rstd[:, 0:SEQ]
        rstd_p = rstd[:, SEQ:SEQ + TT]
        scratch = sb("scratch", [P, 4, GM * SEQ])
        g_sb, s_sb, u_sb, h_sb = [scratch[:, c, :].rearrange("p (m t) -> p m t", m=GM) for c in range(4)]
        q_sb, k_sb = [scratch[:, 2 * c:2 * c + 2, :].rearrange("p b (m t) -> p b m t", m=GM) for c in range(2)]
        pool_u = scratch[:, :, :].rearrange("p g (t e) -> p g t e", t=TT)
        xn = scratch[:, :, :].rearrange("p c (m t) -> p (c m) t", m=GM)
        h_hi = sb("h_hi", [P, 2, GM, SEQ], f32r)
        h_lo = sb("h_lo", [P, 2, GM, SEQ], f32r)
        o_hi = sb("o_hi", [P, DC, SEQ], f32r)
        o_lo = sb("o_lo", [P, DC, SEQ], f32r)
        v_sb = sb("v_sb", [P, 2, TT, GW])
        SC = 3 * P
        dist = sb("dist", [P, SC])
        soft = sb("soft", [P, 3, 2, SC])
        score, prob, probT = [soft[:, c] for c in range(3)]
        sq = soft[:, :, :, :].rearrange("p a b c -> p (a b c)")[:, 0:DC * SEQ].rearrange("p (d t) -> p d t", d=DC)
        neg_max = sb("neg_max", [P, 2, TT])
        row_sum = sb("row_sum", [P, 2, TT])
        row_inv = sb("row_inv", [P, 2, TT])
        band = sb("band", [P, NPG, TT, SEQ])
        count = v_sb[:, :, :, :].rearrange("p b t e -> p (b t) e")
        inv_cnt = count
        x_tok = band[:, :, :, :].rearrange("p (t g) s c -> p t (g s c)", t=TT)

        psum = ctx.enter_context(nc.psum_tensor("psum", [P, 8, 512], f32))

        def bank(b):
            return psum[:, b, :]

        def acc_bank(b):
            return psum[:, b, :].rearrange("p (m t) -> p m t", m=2)

        def y_acc(d):
            return psum[:, 4 + d // 2, (d % 2) * SEQ:(d % 2 + 1) * SEQ]

        raw_loaded = [sem(f"raw_loaded{r}") for r in range(RAW)]
        consts_loaded = sem("consts_loaded")
        x_loaded = sem("x_loaded")
        consts_built = sem("consts_built")
        hi_split = sem("hi_split")
        lo_split = sem("lo_split")
        tile_used = sem("tile_used")
        gate_scaled = sem("gate_scaled")
        up_scaled = sem("up_scaled")
        silu_done = sem("silu_done")
        h_done = sem("h_done")
        h_hi_done = sem("h_hi_done")
        h_lo_done = sem("h_lo_done")
        y_done = sem("y_done")
        x_done = sem("x_done")
        xg_hi_done = sem("xg_hi_done")
        xg_lo_done = sem("xg_lo_done")
        sq_done = sem("sq_done")
        sq_added = sem("sq_added")
        sq_sum_done = sem("sq_sum_done")
        stats_done = sem("stats_done")
        inv_mean_done = sem("inv_mean_done")
        root_done = sem("root_done")
        newton = sem("newton")
        rstd_done = sem("rstd_done")
        gains_T = sem("gains_T")
        gains_done = sem("gains_done")
        qkv_scaled = sem("qkv_scaled")
        score_done = sem("score_done")
        score_biased = sem("score_biased")
        max_done = sem("max_done")
        exp_done = sem("exp_done")
        inv_done = sem("inv_done")
        prob_done = sem("prob_done")
        probT_done = sem("probT_done")
        probT_copied = sem("probT_copied")
        pv_done = sem("pv_done")
        o_hi_done = sem("o_hi_done")
        o_lo_done = sem("o_lo_done")
        pooled = sem("pooled")
        inv_cnt_done = sem("inv_cnt_done")
        xT_last = sem("xT_last")
        pool_u_scaled = sem("pool_u_scaled")
        xn_done = sem("xn_done")
        out_T = sem("out_T")
        out_scaled_act = sem("out_scaled_act")
        out_scaled_dve = sem("out_scaled_dve")
        out_written = sem("out_written")

        gate_v = w_gate.rearrange("l s (k p) f -> l s p k f", p=P)
        up_v = w_up.rearrange("l s (k p) f -> l s p k f", p=P)
        down_v = w_down.rearrange("l s (g m p) d -> l s p g m d", p=P, m=GM)
        qkv_v = w_qkv.rearrange("l (k p) f -> l p k f", p=P)
        wo_v = w_o.rearrange("l (g m p) d -> l p g m d", p=P, m=GM)
        poolw_v = pool_w.rearrange("l g (m p) e -> l p g m e", p=P)

        def col_tile(ring, n):
            return ring[:, n % SPL, :].rearrange("p (k f) -> p k f", k=DC)

        def row_tile(ring, n):
            return ring[:, n % SPL, :].rearrange("p (m d) -> p m d", m=GM)

        GAIN_COL = [0, DC, 2 * DC, 3 * DC, 4 * DC, 5 * DC, 7 * DC]
        POOL_SCALE_COL = 6 * DC

        def gain(norm, d):
            return gains[:, GAIN_COL[norm] + d:GAIN_COL[norm] + d + 1]

        def head_bank(quad, hh):
            return (3, 4, 5, 6)[hh] if quad < QUADS - 1 else (3, 0, 1, 3)[hh]

        def o_bank(quad):
            return 7 if quad < QUADS - 1 else 2

        block = ctx.enter_context(nc.Block())

        @block.sync
        def _(sp):
            sp.dma_start(x_tok[:, :, :], x_in[0].rearrange("(t p) d -> p t d", p=P)).then_inc(x_loaded, 16)
            norms = ln_gains.rearrange("l s (c p) -> (l s c) p", p=P)
            nrows = norms.shape[0]
            sp.dma_start(gains_rows[0:nrows, :], norms).then_inc(consts_loaded, 16)
            sp.dma_start(gains_rows[nrows:nrows + DC, :],
                         pool_scale[0].rearrange("(c p) -> c p", p=P)).then_inc(consts_loaded, 16)
            sp.dma_start(gains_rows[nrows + DC:nrows + 2 * DC, :],
                         final_gain.rearrange("(c p) -> c p", p=P)).then_inc(consts_loaded, 16)

            def load(n, dst_shape, src, i=0):
                sp.wait_ge(lo_split, n + 1 + BODY * i)
                dst = raw[:, n % RAW, :]
                sp.dma_start(dst_shape(dst), src).then_inc(raw_loaded[n % RAW], 16)

            def cols(dst):
                return dst.rearrange("p (k f) -> p k f", k=DC)

            def rows(dst):
                return dst.rearrange("p (m d) -> p m d", m=GM)

            def ffn(n0, layer, side):
                g, u, dn = gate_v[layer, side], up_v[layer, side], down_v[layer, side]
                load(n0, cols, g[:, :, 0:GW])
                load(n0 + 1, cols, u[:, :, 0:GW])
                with sp.Fori(0, PAIRS) as i:
                    for e in range(2):
                        j = 2 * i + (e + 1)
                        load(n0 + 2 + 3 * e, cols, g[:, :, bass.ds(j * GW, GW)], i)
                        load(n0 + 3 + 3 * e, cols, u[:, :, bass.ds(j * GW, GW)], i)
                        load(n0 + 4 + 3 * e, rows, w_down[layer, side, bass.ds((j - 1) * GW, GW), :]
                             .rearrange("(m p) d -> p m d", p=P), i)
                load(n0 + FFN_TILES - 1, rows, dn[:, GROUPS - 1])

            ffn(FFN0, 0, 0)
            for j in range(QUADS):
                for s in range(3):
                    load(ATT0 + 3 * j + s, cols, qkv_v[0][:, :, s * D + j * GW:s * D + (j + 1) * GW])
            for j in range(QUADS):
                load(ATT0 + 3 * QUADS + j, rows, wo_v[0][:, j])
            ffn(FFN1, 0, 1)
            ffn(FFN2, 1, 0)
            load(POOL0, lambda dst: dst.rearrange("p (g m e) -> p g m e", g=NPG, m=GM), poolw_v[0])
            ffn(FFN3, 1, 1)

            out_v = out[0].rearrange("(t p) d -> p t d", p=P)
            for t in range(TT):
                sp.wait_ge(out_scaled_act, t + 1)
                sp.wait_ge(out_scaled_dve, t + 1)
                sp.dma_start(out_v[:, t, :], x_tok[:, t, :]).then_inc(out_written, 16)
            sp.wait_ge(out_written, 16 * TT)

        @block.gpsimd
        def _(pool):
            built = [0]

            def step(ins):
                built[0] += 1
                ins.then_inc(consts_built, 1)
                pool.wait_ge(consts_built, built[0])

            step(pool.memset(ident[:, :], 0.0))
            step(pool.affine_select(out=ident[:, :], in_=ident[:, :], compare_op=ALU.not_equal, fill=1.0,
                                    base=0, pattern=[[-1, P]], channel_multiplier=1))
            step(pool.memset(ones[:, :], 1.0))

            def late_consts():
                for g, w in enumerate(WINDOWS):
                    if g == 0:
                        step(pool.iota(count[:, g, :], [[1, SEQ]], base=1, channel_multiplier=0,
                                       allow_small_or_imprecise_dtypes=True))
                    else:
                        step(pool.tensor_copy(count[:, g, :], count[:, 0, :]))
                for g, w in enumerate(WINDOWS):
                    step(pool.tensor_scalar(count[:, g, :], count[:, g, :], float(w), None, ALU.min))
                for b, base in enumerate((0, P, 0)):
                    blk = dist[:, b * P:(b + 1) * P]
                    step(pool.iota(blk, [[-1, P]], base=base, channel_multiplier=1,
                                   allow_small_or_imprecise_dtypes=True))
                    if base == 0:
                        step(pool.affine_select(out=blk, in_=blk, compare_op=ALU.is_ge, fill=-NEG * 1e4,
                                                base=0, pattern=[[-1, P]], channel_multiplier=1))
                pool.wait_ge(inv_cnt_done, 1)
                pool.wait_ge(x_done, DB)
                for g, w in enumerate(WINDOWS):
                    for st in range(TT):
                        b = band[:, g, st, :]
                        step(pool.affine_select(out=b, in_=inv_cnt[:, g, :], compare_op=ALU.is_ge, fill=0.0,
                                                base=-st * P, pattern=[[1, SEQ]], channel_multiplier=-1))
                        step(pool.affine_select(out=b, in_=b, compare_op=ALU.is_ge, fill=0.0,
                                                base=st * P + w - 1, pattern=[[-1, SEQ]], channel_multiplier=1))
                        step(pool.tensor_tensor(b[:, st * P:(st + 1) * P], b[:, st * P:(st + 1) * P],
                                                ident[:, :], ALU.subtract))

            late_consts()
            assert built[0] == CONSTS

        def gate_tile(j):
            return 3 * j - 1 if j else 0

        def up_tile(j):
            return 3 * j if j else 1

        def down_tile(j):
            return 3 * j + 4 if j < GROUPS - 1 else FFN_TILES - 1

        def used(n, i=0):
            return SPL + n + 1 + BODY * i

        @block.tensor
        def _(pe):
            pe.sem_inc(tile_used, SPL)

            def weights(n, i=0):
                pe.wait_ge(lo_split, RAW + n + 1 + BODY * i)

            def passes(out, hi, lo, rhi, rlo, start, stop):
                nc.tensor.matmul(out, hi, rhi, start=start, stop=False, skip_group_check=True)
                nc.tensor.matmul(out, hi, rlo, start=False, stop=False, skip_group_check=True)
                return nc.tensor.matmul(out, lo, rhi, start=False, stop=stop, skip_group_check=True)

            def column_product(n, b, norm=None):
                hi, lo = col_tile(w_hi, n), col_tile(w_lo, n)
                for k in range(DC):
                    if norm is not None:
                        pe.wait_ge(xg_lo_done, norm * DC + k + 1)
                    for m in range(GM):
                        cols = slice(m * P, (m + 1) * P)
                        last = passes(acc_bank(b)[:, m, :], hi[:, k, cols], lo[:, k, cols],
                                      xg_hi[:, k, :], xg_lo[:, k, :], start=(k == 0 and m == 0), stop=(k == DC - 1))
                last.then_inc(tile_used, 1)

            def row_product(n, src_hi, src_lo, first=False, final=False):
                hi, lo = row_tile(w_hi, n), row_tile(w_lo, n)
                for d in range(DC):
                    for m in range(GM):
                        cols = slice(d * P, (d + 1) * P)
                        last = passes(y_acc(d), hi[:, m, cols], lo[:, m, cols], src_hi[:, m, :], src_lo[:, m, :],
                                      start=(first and m == 0 and d % 2 == 0), stop=(final and m == GM - 1))
                    if final and d % 2 and d < DC - 1:
                        last.then_inc(y_done, 1)
                last.then_inc(tile_used, 1)

            def statistics(norm):
                pe.wait_ge(sq_sum_done, norm + 1)
                nc.tensor.matmul(psum[:, 4, 0:SEQ], ones[:, :], sq_sum[:, :], start=True, stop=True)
                for t in range(TT):
                    last = nc.tensor.matmul(psum[:, 4, SEQ + t:SEQ + t + 1], sq_sum[:, t * P:(t + 1) * P],
                                            ones[:, 0:1], start=True, stop=True)
                last.then_inc(stats_done, 1)

            def ffn(n0, index, norm):
                g0 = index * GROUPS

                def gate_up(j, i=0, static=False):
                    b = 2 * ((g0 + j) % 2)
                    n = n0 + gate_tile(j)
                    weights(n, i)
                    if g0 + j >= 2:
                        pe.wait_ge(gate_scaled, g0 + j - 1 + 2 * i)
                    column_product(n, b, norm if static else None)
                    if static:
                        statistics(norm)
                    n = n0 + up_tile(j)
                    weights(n, i)
                    if g0 + j >= 2:
                        pe.wait_ge(up_scaled, g0 + j - 1 + 2 * i)
                    column_product(n, b + 1)

                def down(j, i=0, first=False, final=False):
                    n = n0 + down_tile(j)
                    weights(n, i)
                    pe.wait_ge(h_lo_done, g0 + j + 1 + 2 * i)
                    hb = (g0 + j) % 2
                    row_product(n, h_hi[:, hb], h_lo[:, hb], first, final)

                gate_up(0, static=True)
                gate_up(1)
                down(0, first=True)
                gate_up(2)
                down(1)
                with pe.Fori(0, PAIRS - 1) as i:
                    gate_up(3, i)
                    down(2, i)
                    gate_up(4, i)
                    down(3, i)
                down(GROUPS - 1, final=True)

            pe.wait_ge(consts_built, 2)
            pe.wait_ge(x_loaded, 16)
            for d in range(DC):
                for t in range(TT):
                    last = nc.tensor.transpose(y_acc(d)[:, t * P:(t + 1) * P], x_tok[:, t, d * P:(d + 1) * P],
                                               ident[:, :])
                if d % 2 and d < DC - 1:
                    last.then_inc(y_done, 1)
            last.then_inc(xT_last, 1)
            pe.wait_ge(consts_loaded, 48)
            nc.tensor.transpose(psum[:, 0, 0:64], gains_rows[:, :], ident[0:64, 0:64]).then_inc(gains_T, 1)
            pe.wait_ge(consts_built, 3)
            pe.wait_ge(gains_done, 1)

            ffn(FFN0, 0, 0)

            def qkv_tile(j, s, norm=None):
                n = ATT0 + 3 * j + s
                weights(n)
                if j:
                    pe.wait_ge(qkv_scaled, 3 * (j - 1) + s + 1)
                elif s == 0:
                    pe.wait_ge(up_scaled, GROUPS)
                if s < 2:
                    column_product(n, s, norm)
                    return
                hi, lo = col_tile(w_hi, n), col_tile(w_lo, n)
                for t in range(TT):
                    toks = slice(t * P, (t + 1) * P)
                    for k in range(DC):
                        out = psum[:, 2, t * GW:(t + 1) * GW]
                        nc.tensor.matmul(out, xg_hi[:, k, toks], hi[:, k, :], start=(k == 0), stop=False,
                                         skip_group_check=True)
                        nc.tensor.matmul(out, xg_hi[:, k, toks], lo[:, k, :], start=False, stop=False,
                                         skip_group_check=True)
                        last = nc.tensor.matmul(out, xg_lo[:, k, toks], hi[:, k, :], start=False, stop=(k == DC - 1),
                                                skip_group_check=True)
                last.then_inc(tile_used, 1)

            def out_tile(j):
                n = ATT0 + 3 * QUADS + j
                weights(n)
                pe.wait_ge(o_lo_done, max(j + 1, QUADS - 1))
                chunks = slice(GM * j, GM * (j + 1))
                row_product(n, o_hi[:, chunks, :], o_lo[:, chunks, :], first=(j == 0), final=(j == QUADS - 1))

            def scores(j, hh):
                H = QH * j + hh
                if hh == 0:
                    pe.wait_ge(qkv_scaled, 3 * (j + 1))
                if H >= QH:
                    pe.wait_ge(probT_copied, H - QH + 1)
                if j == QUADS - 1 and hh == 3:
                    pe.wait_ge(probT_copied, H - 3 + 1)
                s = bank(head_bank(j, hh))
                rows, m = slice(HD * (hh % 2), HD * (hh % 2) + HD), hh // 2
                nc.tensor.matmul(s[:, 0:P], q_sb[rows, j % 2, m, 0:P], k_sb[rows, j % 2, m, 0:P],
                                 start=True, stop=True, skip_group_check=True)
                nc.tensor.matmul(s[:, P:SC], q_sb[rows, j % 2, m, P:SEQ], k_sb[rows, j % 2, m, :],
                                 start=True, stop=True, skip_group_check=True).then_inc(score_done, 1)

            def transposes(j, hh):
                H = QH * j + hh
                pe.wait_ge(prob_done, H + 1)
                s = bank(head_bank(j, hh))
                for b in range(3):
                    last = nc.tensor.transpose(s[:, b * P:(b + 1) * P], prob[:, H % 2, b * P:(b + 1) * P], ident[:, :])
                last.then_inc(probT_done, 1)

            def values(j, hh):
                H = QH * j + hh
                pe.wait_ge(probT_copied, H + 1)
                if hh == 0 and j:
                    pe.wait_ge(o_lo_done, j)
                rows, m = slice(HD * (hh % 2), HD * (hh % 2) + HD), hh // 2
                o = acc_bank(o_bank(j))[rows, m, :]
                chans = slice(hh * HD, (hh + 1) * HD)
                nc.tensor.matmul(o, v_sb[:, j % 2, 0, chans], probT[:, H % 2, 0:SEQ],
                                 start=True, stop=False, skip_group_check=True)
                nc.tensor.matmul(o[:, P:SEQ], v_sb[:, j % 2, 1, chans], probT[:, H % 2, SEQ:SC],
                                 start=False, stop=True, skip_group_check=True).then_inc(pv_done, 1)

            qkv_tile(0, 0, norm=1)
            statistics(1)
            qkv_tile(0, 1)
            qkv_tile(0, 2)
            for j in range(QUADS):
                def between(s):
                    if j < QUADS - 1:
                        qkv_tile(j + 1, s)
                    else:
                        out_tile(s)
                scores(j, 0)
                scores(j, 1)
                between(0)
                transposes(j, 0)
                transposes(j, 1)
                scores(j, 2)
                scores(j, 3)
                between(1)
                values(j, 0)
                values(j, 1)
                transposes(j, 2)
                transposes(j, 3)
                between(2)
                values(j, 2)
                values(j, 3)
            out_tile(QUADS - 1)

            ffn(FFN1, 1, 2)
            ffn(FFN2, 2, 3)

            weights(POOL0)
            pe.wait_ge(up_scaled, 3 * GROUPS)
            whi = w_hi[:, POOL0 % SPL, :].rearrange("p (g m e) -> p g m e", g=NPG, m=GM)
            wlo = w_lo[:, POOL0 % SPL, :].rearrange("p (g m e) -> p g m e", g=NPG, m=GM)
            for g in range(NPG):
                pe.wait_ge(xg_lo_done, 4 * DC + GM * (g + 1))
                for t in range(TT):
                    toks = slice(t * P, (t + 1) * P)
                    for m in range(GM):
                        k = GM * g + m
                        out = psum[:, g, t * GW:(t + 1) * GW]
                        nc.tensor.matmul(out, xg_hi[:, k, toks], whi[:, g, m, :], start=(m == 0), stop=False,
                                         skip_group_check=True)
                        nc.tensor.matmul(out, xg_hi[:, k, toks], wlo[:, g, m, :], start=False, stop=False,
                                         skip_group_check=True)
                        last = nc.tensor.matmul(out, xg_lo[:, k, toks], whi[:, g, m, :], start=False,
                                                stop=(m == GM - 1), skip_group_check=True)
            last.then_inc(tile_used, 1)
            statistics(4)
            pe.wait_ge(consts_built, CONSTS)
            for d in range(DC):
                g, m = d // GM, d % GM
                if m == 0:
                    pe.wait_ge(pool_u_scaled, g + 1)
                nc.tensor.matmul(y_acc(d), pool_u[:, g, 0, m * P:(m + 1) * P], band[:, g, 0, :],
                                 start=(d % 2 == 0), stop=False, skip_group_check=True)
                last = nc.tensor.matmul(y_acc(d)[:, P:SEQ], pool_u[:, g, 1, m * P:(m + 1) * P], band[:, g, 1, P:SEQ],
                                        start=False, stop=True, skip_group_check=True)
                if d % 2 and d < DC - 1:
                    last.then_inc(y_done, 1)
            last.then_inc(pooled, 1)

            ffn(FFN3, 3, 5)

            pe.wait_ge(up_scaled, 4 * GROUPS)
            for d in range(DC):
                pe.wait_ge(xn_done, d + 1)
                for t in range(TT):
                    last = nc.tensor.transpose(psum[:, 2 * t + d // 4, (d % 4) * P:(d % 4 + 1) * P],
                                               xn[:, d, t * P:(t + 1) * P], ident[:, :])
            last.then_inc(out_T, 1)
            statistics(6)

        def wait_pair(eng, norm, c):
            if c < DB - 1:
                eng.wait_ge(y_done, norm * (DB - 1) + c + 1)
            elif norm == 0:
                eng.wait_ge(xT_last, 1)
            elif norm == 5:
                eng.wait_ge(pooled, 1)
            else:
                eng.wait_ge(tile_used, used({1: ATT0, 2: FFN1, 3: FFN2, 4: POOL0, 6: TILES}[norm] - 1))

        def group_tiles(n0, j):
            return range(n0 + 3 * j + 3, n0 + 3 * j + 6)

        @block.scalar
        def _(act):
            def split_hi(n, i=0):
                if n >= TILES:
                    return
                act.wait_ge(raw_loaded[n % RAW], 16 * (n // RAW + 1) + 16 * (BODY // RAW) * i)
                act.wait_ge(tile_used, n + 1 + BODY * i)
                nc.scalar.activation(w_hi[:, n % SPL, :], raw[:, n % RAW, :], ACT.Copy).then_inc(hi_split, 1)

            def round_x(norm):
                for d in range(DC):
                    act.wait_ge(x_done, norm * DB + d // 2 + 1)
                    nc.scalar.activation(xg_hi[:, d, :], x[:, d, :], ACT.Copy,
                                         scale=gain(norm, d)).then_inc(xg_hi_done, 1)

            def squares(norm):
                for c in range(DB):
                    act.wait_ge(x_done, norm * DB + c + 1)
                    pair = slice(2 * c, 2 * c + 2)
                    nc.scalar.activation(sq[:, pair, :], x[:, pair, :], ACT.Square).then_inc(sq_done, 1)

            def root(norm):
                act.wait_ge(inv_mean_done, norm + 1)
                nc.scalar.activation(rstd[:, :], rstd[:, :], ACT.Sqrt).then_inc(root_done, 1)

            def ffn(n0, index, norm, next_norm):
                g0 = index * GROUPS
                root(norm)

                def step(j, i=0):
                    a, b, c = group_tiles(n0, j)
                    split_hi(a, i)
                    act.wait_ge(gate_scaled, g0 + j + 1 + 2 * i)
                    nc.scalar.activation(s_sb, g_sb, ACT.Silu).then_inc(silu_done, 1)
                    split_hi(b, i)
                    act.wait_ge(h_done, g0 + j + 1 + 2 * i)
                    nc.scalar.activation(h_hi[:, (g0 + j) % 2], h_sb, ACT.Copy).then_inc(h_hi_done, 1)
                    split_hi(c, i)

                with act.Fori(0, PAIRS) as i:
                    step(0, i)
                    step(1, i)
                step(GROUPS - 1)
                if next_norm is not None:
                    round_x(next_norm)
                    squares(next_norm)

            act.wait_ge(gains_done, 1)
            round_x(0)
            split_hi(0)
            squares(0)
            split_hi(1)
            split_hi(2)
            ffn(FFN0, 0, 0, 1)

            def exps(H):
                b = H % 2
                act.wait_ge(max_done, H + 1)
                nc.scalar.activation(prob[:, b, 0:P], score[:, b, 0:P], ACT.Exp, bias=neg_max[:, b, 0:1],
                                     accum_out=row_sum[:, b, 0:1])
                nc.scalar.activation(prob[:, b, P:SC], score[:, b, P:SC], ACT.Exp, bias=neg_max[:, b, 1:2],
                                     accum_out=row_sum[:, b, 1:2]).then_inc(exp_done, 1)

            def normalise(H):
                b = H % 2
                act.wait_ge(exp_done, H + 1)
                act.wait_ge(inv_done, H + 1)
                nc.scalar.activation(prob[:, b, 0:P], prob[:, b, 0:P], ACT.Copy, scale=row_inv[:, b, 0:1])
                nc.scalar.activation(prob[:, b, P:SC], prob[:, b, P:SC], ACT.Copy,
                                     scale=row_inv[:, b, 1:2]).then_inc(prob_done, 1)

            def copy_probT(j, hh):
                H = QH * j + hh
                act.wait_ge(probT_done, H + 1)
                nc.scalar.activation(probT[:, H % 2, :], bank(head_bank(j, hh))[:, 0:SC],
                                     ACT.Copy).then_inc(probT_copied, 1)

            root(1)
            for n in range(3, 6):
                split_hi(ATT0 + n)
            for j in range(QUADS):
                for half in range(2):
                    heads = (2 * half, 2 * half + 1)
                    for hh in heads:
                        exps(QH * j + hh)
                    split_hi(ATT0 + 6 + 3 * j + half)
                    for hh in heads:
                        normalise(QH * j + hh)
                    for hh in heads:
                        copy_probT(j, hh)
                split_hi(ATT0 + 8 + 3 * j)
                act.wait_ge(pv_done, QH * (j + 1))
                nc.scalar.activation(o_hi[:, GM * j:GM * (j + 1), :], acc_bank(o_bank(j)),
                                     ACT.Copy).then_inc(o_hi_done, 1)
            split_hi(ATT0 + 18)
            round_x(2)
            squares(2)

            ffn(FFN1, 1, 2, 3)
            ffn(FFN2, 2, 3, 4)
            root(4)
            split_hi(FFN3 + 2)
            for g in range(NPG):
                act.wait_ge(rstd_done, 5)
                act.wait_ge(tile_used, used(POOL0))
                for t in range(TT):
                    last = nc.scalar.activation(pool_u[:, g, t, :], psum[:, g, t * GW:(t + 1) * GW], ACT.Copy,
                                                scale=rstd_p[:, t:t + 1])
                last.then_inc(pool_u_scaled, 1)
            round_x(5)
            squares(5)
            ffn(FFN3, 3, 5, None)

            for d in range(DC):
                act.wait_ge(x_done, 6 * DB + d // 2 + 1)
                nc.scalar.activation(xn[:, d, :], x[:, d, :], ACT.Copy, scale=gain(6, d)).then_inc(xn_done, 1)
            squares(6)
            root(6)
            act.wait_ge(out_T, 1)
            act.wait_ge(rstd_done, 7)
            for t in range(TT):
                nc.scalar.activation(x_tok[:, t, 0:512], bank(2 * t), ACT.Copy,
                                     scale=rstd_p[:, t:t + 1]).then_inc(out_scaled_act, 1)

        @block.vector
        def _(dve):
            dve.sem_inc(lo_split, RAW)

            def split_lo(n, i=0):
                if n >= TILES:
                    return
                dve.wait_ge(hi_split, n + 1 + BODY * i)
                nc.vector.tensor_tensor(w_lo[:, n % SPL, :], raw[:, n % RAW, :], w_hi[:, n % SPL, :].bitcast(f32),
                                        ALU.subtract).then_inc(lo_split, 1)

            def update_x(norm, scalar=None, split=True, per_chunk=False):
                for c in range(DB + 1):
                    if c < DB:
                        wait_pair(dve, norm, c)
                        pair = acc_bank(4 + c)
                        xs = x[:, 2 * c:2 * c + 2, :]
                        if norm == 0:
                            ins = nc.vector.tensor_copy(xs, pair)
                        elif per_chunk:
                            for e in range(2):
                                ins = nc.vector.scalar_tensor_tensor(out=xs[:, e, :], in0=pair[:, e, :],
                                                                     scalar=scalar(2 * c + e), in1=xs[:, e, :],
                                                                     op0=ALU.mult, op1=ALU.add)
                        else:
                            ins = nc.vector.scalar_tensor_tensor(out=xs, in0=pair, scalar=scalar, in1=xs,
                                                                 op0=ALU.mult, op1=ALU.add)
                        ins.then_inc(x_done, 1)
                    if c and split:
                        for d in (2 * c - 2, 2 * c - 1):
                            dve.wait_ge(xg_hi_done, norm * DC + d + 1)
                            nc.vector.scalar_tensor_tensor(out=xg_lo[:, d, :], in0=x[:, d, :], scalar=gain(norm, d),
                                                           in1=xg_hi[:, d, :].bitcast(f32),
                                                           op0=ALU.mult, op1=ALU.subtract).then_inc(xg_lo_done, 1)

            def newton_step(ins):
                steps[0] += 1
                ins.then_inc(newton, 1)
                dve.wait_ge(newton, steps[0])

            steps = [0]

            def sum_squares(norm):
                for c in range(1, DB):
                    dve.wait_ge(sq_done, norm * DB + c + 1)
                    if c > 1:
                        dve.wait_ge(sq_added, norm * (DB - 1) + c - 1)
                    nc.vector.tensor_tensor(sq[:, 0:2, :], sq[:, 0:2, :], sq[:, 2 * c:2 * c + 2, :],
                                            ALU.add).then_inc(sq_added, 1)
                dve.wait_ge(sq_added, (norm + 1) * (DB - 1))
                nc.vector.tensor_tensor(sq_sum[:, :], sq[:, 0, :], sq[:, 1, :], ALU.add).then_inc(sq_sum_done, 1)

            def rsqrt_mean(norm):
                dve.wait_ge(stats_done, norm + 1)
                newton_step(nc.vector.tensor_scalar(mean[:, :], psum[:, 4, 0:SEQ + TT], 1.0 / D, EPS,
                                                    ALU.mult, ALU.add))
                nc.vector.reciprocal(rstd[:, :], mean[:, :]).then_inc(inv_mean_done, 1)
                dve.wait_ge(root_done, norm + 1)
                newton_step(nc.vector.tensor_tensor(rms_sq[:, :], rstd[:, :], rstd[:, :], ALU.mult))
                newton_step(nc.vector.scalar_tensor_tensor(out=rms_sq[:, :], in0=rms_sq[:, :], scalar=-0.5,
                                                           in1=mean[:, :], op0=ALU.mult, op1=ALU.mult))
                nc.vector.scalar_tensor_tensor(out=rstd[:, :], in0=rms_sq[:, :], scalar=1.5, in1=rstd[:, :],
                                               op0=ALU.add, op1=ALU.mult).then_inc(rstd_done, 1)

            rstd_m = rstd_t.unsqueeze(1).broadcast_to([P, GM, SEQ])

            def ffn(n0, index, norm):
                g0 = index * GROUPS

                def step(j, i=0):
                    a, b, c = group_tiles(n0, j)
                    gate_n, up_n = n0 + gate_tile(j), n0 + up_tile(j)
                    dve.wait_ge(tile_used, used(gate_n, i))
                    if j == 0:
                        dve.wait_ge(rstd_done, norm + 1)
                    nc.vector.tensor_tensor(g_sb, acc_bank(2 * ((g0 + j) % 2)), rstd_m, ALU.mult).then_inc(gate_scaled, 1)
                    dve.wait_ge(tile_used, used(up_n, i))
                    nc.vector.tensor_tensor(u_sb, acc_bank(2 * ((g0 + j) % 2) + 1), rstd_m,
                                            ALU.mult).then_inc(up_scaled, 1)
                    split_lo(a, i)
                    dve.wait_ge(silu_done, g0 + j + 1 + 2 * i)
                    dve.wait_ge(up_scaled, g0 + j + 1 + 2 * i)
                    nc.vector.tensor_tensor(h_sb, s_sb, u_sb, ALU.mult).then_inc(h_done, 1)
                    split_lo(b, i)
                    dve.wait_ge(h_hi_done, g0 + j + 1 + 2 * i)
                    nc.vector.tensor_tensor(h_lo[:, (g0 + j) % 2], h_sb, h_hi[:, (g0 + j) % 2].bitcast(f32),
                                            ALU.subtract).then_inc(h_lo_done, 1)
                    split_lo(c, i)

                rsqrt_mean(norm)
                step(0)
                with dve.Fori(0, PAIRS - 1) as i:
                    step(1, i)
                    step(2, i)
                step(GROUPS - 2)
                step(GROUPS - 1)

            dve.wait_ge(gains_T, 1)
            nc.vector.tensor_copy(gains[:, :], psum[:, 0, 0:64]).then_inc(gains_done, 1)
            dve.wait_ge(gains_done, 1)
            dve.wait_ge(consts_built, COUNTS)
            nc.vector.reciprocal(inv_cnt[:, :, :], count[:, :, :]).then_inc(inv_cnt_done, 1)
            update_x(0)
            split_lo(0)
            sum_squares(0)
            split_lo(1)
            split_lo(2)
            ffn(FFN0, 0, 0)
            update_x(1, 0.5)
            sum_squares(1)

            def qkv_scale(j, s):
                dve.wait_ge(tile_used, used(ATT0 + 3 * j + s))
                if s == 0:
                    ins = nc.vector.scalar_tensor_tensor(out=q_sb[:, j % 2], in0=acc_bank(0), scalar=HD ** -0.5,
                                                         in1=rstd_m, op0=ALU.mult, op1=ALU.mult)
                elif s == 1:
                    ins = nc.vector.tensor_tensor(k_sb[:, j % 2], acc_bank(1), rstd_m, ALU.mult)
                else:
                    for t in range(TT):
                        ins = nc.vector.tensor_scalar(v_sb[:, j % 2, t, :], psum[:, 2, t * GW:(t + 1) * GW],
                                                      rstd_p[:, t:t + 1], None, ALU.mult)
                ins.then_inc(qkv_scaled, 1)

            def bias_and_max(j, hh):
                H = QH * j + hh
                b = H % 2
                slope = 2.0 ** (-8.0 * (H + 1) / HEADS)
                dve.wait_ge(score_done, H + 1)
                nc.vector.scalar_tensor_tensor(out=score[:, b, :], in0=dist[:, :], scalar=-slope,
                                               in1=bank(head_bank(j, hh))[:, 0:SC], op0=ALU.mult,
                                               op1=ALU.add).then_inc(score_biased, 1)
                dve.wait_ge(score_biased, H + 1)
                nc.vector.tensor_reduce(neg_max[:, b, 0:1], score[:, b, 0:P], AX.X, ALU.max, negate=True)
                nc.vector.tensor_reduce(neg_max[:, b, 1:2], score[:, b, P:SC], AX.X, ALU.max,
                                        negate=True).then_inc(max_done, 1)

            def invert(H):
                dve.wait_ge(exp_done, H + 1)
                nc.vector.reciprocal(row_inv[:, H % 2, :], row_sum[:, H % 2, :]).then_inc(inv_done, 1)

            rsqrt_mean(1)
            dve.wait_ge(consts_built, CONSTS)
            dve.wait_ge(rstd_done, 2)
            for s in range(3):
                qkv_scale(0, s)
                split_lo(ATT0 + 3 + s)
            for j in range(QUADS):
                for half in range(2):
                    heads = (2 * half, 2 * half + 1)
                    for hh in heads:
                        bias_and_max(j, hh)
                    split_lo(ATT0 + 6 + 3 * j + half)
                    for hh in heads:
                        invert(QH * j + hh)
                    if j < QUADS - 1:
                        qkv_scale(j + 1, half)
                split_lo(ATT0 + 8 + 3 * j)
                if j < QUADS - 1:
                    qkv_scale(j + 1, 2)
                dve.wait_ge(o_hi_done, j + 1)
                nc.vector.tensor_tensor(o_lo[:, GM * j:GM * (j + 1), :], acc_bank(o_bank(j)),
                                        o_hi[:, GM * j:GM * (j + 1), :].bitcast(f32),
                                        ALU.subtract).then_inc(o_lo_done, 1)
            split_lo(ATT0 + 18)
            update_x(2, 1.0)
            sum_squares(2)

            ffn(FFN1, 1, 2)
            update_x(3, 0.5)
            sum_squares(3)
            ffn(FFN2, 2, 3)
            update_x(4, 0.5)
            sum_squares(4)
            rsqrt_mean(4)
            split_lo(FFN3 + 2)
            update_x(5, lambda d: gains[:, POOL_SCALE_COL + d:POOL_SCALE_COL + d + 1], per_chunk=True)
            sum_squares(5)
            ffn(FFN3, 3, 5)
            update_x(6, 0.5, split=False)
            sum_squares(6)
            rsqrt_mean(6)
            dve.wait_ge(out_T, 1)
            dve.wait_ge(rstd_done, 7)
            for t in range(TT):
                nc.vector.tensor_scalar(x_tok[:, t, 512:1024], bank(2 * t + 1), rstd_p[:, t:t + 1], None,
                                        ALU.mult).then_inc(out_scaled_dve, 1)


_INS = ["x", "ln_gains", "ffn_w_gate", "ffn_w_up", "ffn_w_down", "attn_w_qkv", "attn_w_o", "pool_w", "pool_scale",
        "final_gain"]


def kernel(**inputs):
    import numpy as np
    import concourse.bacc as bacc
    from concourse.bass_utils import run_bass_kernel_spmd

    nc = bacc.Bacc("TRN2", target_bir_lowering=False, num_devices=1)
    arrays, args = {}, []
    for name in _INS:
        a = np.ascontiguousarray(inputs[name])
        arrays[f"in_{name}_dram"] = a
        args.append(nc.dram_tensor(f"in_{name}_dram", a.shape, mybir.dt.from_np(a.dtype), kind="ExternalInput").ap())
    shape = inputs["x"].shape
    out = nc.dram_tensor("out_dram", shape, mybir.dt.float32, kind="ExternalOutput").ap()
    build_trunk(nc, *args, out)
    r = run_bass_kernel_spmd(nc, [arrays], core_ids=[0])
    return r.results[0]["out_dram"]
```

```python
from contextlib import ExitStack

import concourse.bass as bass
from concourse import mybir


def build_trunk(nc, x_in, ln_gains, w_gate, w_up, w_down, w_qkv, w_o, pool_w, pool_scale, final_gain, out):
    f32 = mybir.dt.float32
    f32r = mybir.dt.float32r
    ALU = mybir.AluOpType
    ACT = mybir.ActivationFunctionType
    AX = mybir.AxisListType

    P = 128
    SEQ, D = x_in.shape[1], x_in.shape[2]
    F = w_gate.shape[3]
    DC = D // P
    TT = SEQ // P
    DB = DC // 2
    GW = 256
    GM = GW // P
    GROUPS = F // GW
    HD = 64
    HEADS = D // HD
    QH = GW // HD
    QUADS = HEADS // QH
    WINDOWS = (2, 4, 8, 16)
    NPG = len(WINDOWS)
    EPS = 1e-6
    NEG = -1e30
    ROWS = DC * GW
    RAW = 3
    SPL = 6
    BODY = 6
    assert GROUPS % 2 == 1 and F % GW == 0 and SEQ == 2 * P and GM * D == ROWS and SPL == BODY and BODY % RAW == 0
    PAIRS = (GROUPS - 1) // 2
    FFN_TILES = 3 * GROUPS
    ATT_TILES = 4 * QUADS

    COUNTS = 3 + 3 * NPG
    CONSTS = COUNTS + 1 + 5 + NPG * 3 * TT

    FFN0, ATT0, FFN1 = 0, FFN_TILES, FFN_TILES + ATT_TILES
    FFN2 = FFN1 + FFN_TILES
    POOL0 = FFN2 + FFN_TILES
    FFN3 = POOL0 + 1
    TILES = FFN3 + FFN_TILES

    ctx = ExitStack()
    with ctx:
        def sb(name, shape, dt=f32):
            return ctx.enter_context(nc.sbuf_tensor(name, shape, dt))

        def sem(name):
            return ctx.enter_context(nc.semaphore(name))

        raw = sb("raw", [P, RAW, ROWS])
        w_hi = sb("w_hi", [P, SPL, ROWS], f32r)
        w_lo = sb("w_lo", [P, SPL, ROWS], f32r)
        x = sb("x", [P, DC, SEQ])
        xg_hi = sb("xg_hi", [P, DC, SEQ], f32r)
        xg_lo = sb("xg_lo", [P, DC, SEQ], f32r)
        gains_rows = sb("gains_rows", [64, P])
        gains = sb("gains", [P, 64])
        ident = sb("ident", [P, P])
        ones = sb("ones", [P, P])
        sq_sum = sb("sq_sum", [P, SEQ])
        mean = sb("mean", [P, SEQ + TT])
        rms_sq = sb("rms_sq", [P, SEQ + TT])
        rstd = sb("rstd", [P, SEQ + TT])
        rstd_t = rstd[:, 0:SEQ]
        rstd_p = rstd[:, SEQ:SEQ + TT]
        scratch = sb("scratch", [P, 4, GM * SEQ])
        g_sb, s_sb, u_sb, h_sb = [scratch[:, c, :].rearrange("p (m t) -> p m t", m=GM) for c in range(4)]
        q_sb, k_sb = [scratch[:, 2 * c:2 * c + 2, :].rearrange("p b (m t) -> p b m t", m=GM) for c in range(2)]
        pool_u = scratch[:, :, :].rearrange("p g (t e) -> p g t e", t=TT)
        xn = scratch[:, :, :].rearrange("p c (m t) -> p (c m) t", m=GM)
        h_hi = sb("h_hi", [P, 2, GM, SEQ], f32r)
        h_lo = sb("h_lo", [P, 2, GM, SEQ], f32r)
        o_hi = sb("o_hi", [P, DC, SEQ], f32r)
        o_lo = sb("o_lo", [P, DC, SEQ], f32r)
        v_sb = sb("v_sb", [P, 2, TT, GW])
        SC = 3 * P
        dist = sb("dist", [P, SC])
        soft = sb("soft", [P, 3, 2, SC])
        score, prob, probT = [soft[:, c] for c in range(3)]
        sq = soft[:, :, :, :].rearrange("p a b c -> p (a b c)")[:, 0:DC * SEQ].rearrange("p (d t) -> p d t", d=DC)
        neg_max = sb("neg_max", [P, 2, TT])
        row_sum = sb("row_sum", [P, 2, TT])
        row_inv = sb("row_inv", [P, 2, TT])
        band = sb("band", [P, NPG, TT, SEQ])
        inv_cnt = v_sb[:, :, :, :].rearrange("p b t e -> p (b t) e")
        count = sb("count", [P, NPG, WINDOWS[-1]])
        x_tok = band[:, :, :, :].rearrange("p (t g) s c -> p t (g s c)", t=TT)

        psum = ctx.enter_context(nc.psum_tensor("psum", [P, 8, 512], f32))

        def bank(b):
            return psum[:, b, :]

        def acc_bank(b):
            return psum[:, b, :].rearrange("p (m t) -> p m t", m=2)

        def y_acc(d):
            return psum[:, 4 + d // 2, (d % 2) * SEQ:(d % 2 + 1) * SEQ]

        raw_loaded = [sem(f"raw_loaded{r}") for r in range(RAW)]
        consts_loaded = sem("consts_loaded")
        x_loaded = [sem(f"x_loaded{c}") for c in range(2)]
        piece_loaded = [sem(f"piece_loaded{c}") for c in range(DB - 1)]
        piece_hi = sem("piece_hi")
        warm = sem("warm")
        piece_lo = sem("piece_lo")
        consts_built = sem("consts_built")
        hi_split = sem("hi_split")
        lo_split = sem("lo_split")
        tile_used = sem("tile_used")
        gate_scaled = sem("gate_scaled")
        up_scaled = sem("up_scaled")
        silu_done = sem("silu_done")
        h_done = sem("h_done")
        h_hi_done = sem("h_hi_done")
        h_lo_done = sem("h_lo_done")
        y_done = sem("y_done")
        x_done = sem("x_done")
        xg_hi_done = sem("xg_hi_done")
        xg_lo_done = sem("xg_lo_done")
        sq_done = sem("sq_done")
        sq_added = sem("sq_added")
        sq_sum_done = sem("sq_sum_done")
        stats_done = sem("stats_done")
        inv_mean_done = sem("inv_mean_done")
        root_done = sem("root_done")
        newton = sem("newton")
        rstd_done = sem("rstd_done")
        gains_T = sem("gains_T")
        gains_done = sem("gains_done")
        qkv_scaled = sem("qkv_scaled")
        score_done = sem("score_done")
        score_biased = sem("score_biased")
        max_done = sem("max_done")
        exp_done = sem("exp_done")
        inv_done = sem("inv_done")
        prob_done = sem("prob_done")
        probT_done = sem("probT_done")
        probT_copied = sem("probT_copied")
        pv_done = sem("pv_done")
        o_hi_done = sem("o_hi_done")
        o_lo_done = sem("o_lo_done")
        pooled = sem("pooled")
        inv_cnt_done = sem("inv_cnt_done")
        xT_last = sem("xT_last")
        pool_u_scaled = sem("pool_u_scaled")
        xn_done = sem("xn_done")
        out_T = sem("out_T")
        out_scaled_act = sem("out_scaled_act")
        out_scaled_dve = sem("out_scaled_dve")
        out_written = sem("out_written")

        gate_v = w_gate.rearrange("l s (k p) f -> l s p k f", p=P)
        up_v = w_up.rearrange("l s (k p) f -> l s p k f", p=P)
        down_v = w_down.rearrange("l s (g m p) d -> l s p g m d", p=P, m=GM)
        qkv_v = w_qkv.rearrange("l (k p) f -> l p k f", p=P)
        wo_v = w_o.rearrange("l (g m p) d -> l p g m d", p=P, m=GM)
        poolw_v = pool_w.rearrange("l g (m p) e -> l p g m e", p=P)

        def col_tile(ring, n):
            return ring[:, n % SPL, :].rearrange("p (k f) -> p k f", k=DC)

        def row_tile(ring, n):
            return ring[:, n % SPL, :].rearrange("p (m d) -> p m d", m=GM)

        GAIN_COL = [0, DC, 2 * DC, 3 * DC, 4 * DC, 5 * DC, 7 * DC]
        POOL_SCALE_COL = 6 * DC

        def gain(norm, d):
            return gains[:, GAIN_COL[norm] + d:GAIN_COL[norm] + d + 1]

        def head_bank(quad, hh):
            return (3, 4, 5, 6)[hh] if quad < QUADS - 1 else (3, 0, 1, 3)[hh]

        def o_bank(quad):
            return 7 if quad < QUADS - 1 else 2

        def loop(eng, turns):
            return nc.Fori(0, turns, engines=[eng.engine], hint_back_edge=True)

        block = ctx.enter_context(nc.Block())

        @block.sync
        def _(sp):
            x_v = x_in[0].rearrange("(t p) d -> p t d", p=P)
            for c in range(2):
                half = slice(c * D // 2, (c + 1) * D // 2)
                sp.dma_start(x_tok[:, :, half], x_v[:, :, half]).then_inc(x_loaded[c], 16)

            def load(n, dst_shape, src, i=0):
                sp.wait_ge(lo_split, n + 1 + BODY * i)
                dst = raw[:, n % RAW, :]
                sp.dma_start(dst_shape(dst), src).then_inc(raw_loaded[n % RAW], 16)

            def cols(dst):
                return dst.rearrange("p (k f) -> p k f", k=DC)

            def rows(dst):
                return dst.rearrange("p (m d) -> p m d", m=GM)

            def ffn(n0, layer, side):
                g, u, dn = gate_v[layer, side], up_v[layer, side], down_v[layer, side]
                if n0 == FFN0:
                    for c in range(DB):
                        pair = slice(2 * c, 2 * c + 2)
                        sp.dma_start(cols(raw[:, 0, :])[:, pair, :], g[:, pair, 0:GW]) \
                          .then_inc(piece_loaded[c] if c < DB - 1 else raw_loaded[0], 16)
                else:
                    load(n0, cols, g[:, :, 0:GW])
                load(n0 + 1, cols, u[:, :, 0:GW])
                with loop(sp, PAIRS) as i:
                    for e in range(2):
                        j = 2 * i + (e + 1)
                        load(n0 + 2 + 3 * e, cols, g[:, :, bass.ds(j * GW, GW)], i)
                        load(n0 + 3 + 3 * e, cols, u[:, :, bass.ds(j * GW, GW)], i)
                        load(n0 + 4 + 3 * e, rows, w_down[layer, side, bass.ds((j - 1) * GW, GW), :]
                             .rearrange("(m p) d -> p m d", p=P), i)
                load(n0 + FFN_TILES - 1, rows, dn[:, GROUPS - 1])

            ffn(FFN0, 0, 0)
            for j in range(QUADS):
                for s in range(3):
                    load(ATT0 + 3 * j + s, cols, qkv_v[0][:, :, s * D + j * GW:s * D + (j + 1) * GW])
            for j in range(QUADS):
                load(ATT0 + 3 * QUADS + j, rows, wo_v[0][:, j])
            ffn(FFN1, 0, 1)
            ffn(FFN2, 1, 0)
            load(POOL0, lambda dst: dst.rearrange("p (g m e) -> p g m e", g=NPG, m=GM), poolw_v[0])
            ffn(FFN3, 1, 1)

            out_v = out[0].rearrange("(t p) d -> p t d", p=P)
            for t in range(TT):
                sp.wait_ge(out_scaled_act, t + 1)
                sp.wait_ge(out_scaled_dve, t + 1)
                sp.dma_start(out_v[:, t, :], x_tok[:, t, :]).then_inc(out_written, 16)
            sp.wait_ge(out_written, 16 * TT)

        @block.gpsimd
        def _(pool):
            built = [0]

            def step(ins):
                built[0] += 1
                ins.then_inc(consts_built, 1)
                pool.wait_ge(consts_built, built[0])

            step(pool.memset(ident[:, :], 0.0))
            step(pool.affine_select(out=ident[:, :], in_=ident[:, :], compare_op=ALU.not_equal, fill=1.0,
                                    base=0, pattern=[[-1, P]], channel_multiplier=1))
            step(pool.memset(ones[:, :], 1.0))

            def late_consts():
                for g, w in enumerate(WINDOWS):
                    step(pool.iota(count[:, g, :], [[1, WINDOWS[-1]]], base=1, channel_multiplier=0,
                                   allow_small_or_imprecise_dtypes=True))
                    step(pool.tensor_scalar(count[:, g, :], count[:, g, :], float(w), None, ALU.min))
                    step(pool.memset(inv_cnt[:, g, :], 1.0 / w))
                pool.wait_ge(inv_cnt_done, 1)
                step(pool.tensor_copy(inv_cnt[:, :, 0:WINDOWS[-1]], count[:, :, :]))
                for b, base in enumerate((0, P, 0)):
                    blk = dist[:, b * P:(b + 1) * P]
                    step(pool.iota(blk, [[-1, P]], base=base, channel_multiplier=1,
                                   allow_small_or_imprecise_dtypes=True))
                    if base == 0:
                        step(pool.affine_select(out=blk, in_=blk, compare_op=ALU.is_ge, fill=-NEG * 1e4,
                                                base=0, pattern=[[-1, P]], channel_multiplier=1))
                pool.wait_ge(x_done, DB)
                for g, w in enumerate(WINDOWS):
                    for st in range(TT):
                        b = band[:, g, st, :]
                        step(pool.affine_select(out=b, in_=inv_cnt[:, g, :], compare_op=ALU.is_ge, fill=0.0,
                                                base=-st * P, pattern=[[1, SEQ]], channel_multiplier=-1))
                        step(pool.affine_select(out=b, in_=b, compare_op=ALU.is_ge, fill=0.0,
                                                base=st * P + w - 1, pattern=[[-1, SEQ]], channel_multiplier=1))
                        step(pool.tensor_tensor(b[:, st * P:(st + 1) * P], b[:, st * P:(st + 1) * P],
                                                ident[:, :], ALU.subtract))

            late_consts()
            assert built[0] == CONSTS

        def gate_tile(j):
            return 3 * j - 1 if j else 0

        def up_tile(j):
            return 3 * j if j else 1

        def down_tile(j):
            return 3 * j + 4 if j < GROUPS - 1 else FFN_TILES - 1

        def used(n, i=0):
            return SPL + n + 1 + BODY * i

        @block.tensor
        def _(pe):
            pe.sem_inc(tile_used, SPL)

            def weights(n, i=0):
                pe.wait_ge(lo_split, RAW + n + 1 + BODY * i)

            def passes(out, hi, lo, rhi, rlo, start, stop):
                nc.tensor.matmul(out, hi, rhi, start=start, stop=False, skip_group_check=True)
                nc.tensor.matmul(out, hi, rlo, start=False, stop=False, skip_group_check=True)
                return nc.tensor.matmul(out, lo, rhi, start=False, stop=stop, skip_group_check=True)

            def statistics(norm):
                pe.wait_ge(sq_sum_done, norm + 1)
                if norm not in (4, 6):
                    nc.tensor.matmul(psum[:, 4, 0:SEQ], ones[:, :], sq_sum[:, :], start=True, stop=True)
                for t in range(TT):
                    last = nc.tensor.matmul(psum[:, 4, SEQ + t:SEQ + t + 1], sq_sum[:, t * P:(t + 1) * P],
                                            ones[:, 0:1], start=True, stop=True)
                last.then_inc(stats_done, 1)

            def column_product(n, b, norm=None, stats_norm=None):
                hi, lo = col_tile(w_hi, n), col_tile(w_lo, n)
                for k in range(DC):
                    if norm is not None:
                        pe.wait_ge(xg_lo_done, norm * DC + k + 1)
                    if n == FFN0:
                        if k < DC - 2:
                            pe.wait_ge(piece_lo, k // 2 + 1)
                        else:
                            pe.wait_ge(lo_split, RAW + 1)
                    if stats_norm is not None and k == DC // 2:
                        statistics(stats_norm)
                    for m in range(GM):
                        cols = slice(m * P, (m + 1) * P)
                        last = passes(acc_bank(b)[:, m, :], hi[:, k, cols], lo[:, k, cols],
                                      xg_hi[:, k, :], xg_lo[:, k, :], start=(k == 0 and m == 0), stop=(k == DC - 1))
                last.then_inc(tile_used, 1)

            def row_product(n, src_hi, src_lo, first=False, final=False, halfway=None):
                hi, lo = row_tile(w_hi, n), row_tile(w_lo, n)
                for d in range(DC):
                    if halfway and d == DC // 2:
                        halfway()
                    for m in range(GM):
                        cols = slice(d * P, (d + 1) * P)
                        last = passes(y_acc(d), hi[:, m, cols], lo[:, m, cols], src_hi[:, m, :], src_lo[:, m, :],
                                      start=(first and m == 0 and d % 2 == 0), stop=(final and m == GM - 1))
                    if final and d % 2 and d < DC - 1:
                        last.then_inc(y_done, 1)
                last.then_inc(tile_used, 1)

            def ffn(n0, index, norm):
                g0 = index * GROUPS

                def gate_up(j, i=0, static=False):
                    b = 2 * ((g0 + j) % 2)
                    n = n0 + gate_tile(j)
                    if n != FFN0:
                        weights(n, i)
                    if g0 + j >= 2:
                        pe.wait_ge(gate_scaled, g0 + j - 1 + 2 * i)
                    column_product(n, b, norm if static else None)
                    n = n0 + up_tile(j)
                    weights(n, i)
                    if g0 + j >= 2:
                        pe.wait_ge(up_scaled, g0 + j - 1 + 2 * i)
                    column_product(n, b + 1, stats_norm=norm if static else None)

                def down(j, i=0, first=False, final=False):
                    n = n0 + down_tile(j)
                    weights(n, i)
                    pe.wait_ge(h_lo_done, g0 + j + 1 + 2 * i)
                    hb = (g0 + j) % 2
                    row_product(n, h_hi[:, hb], h_lo[:, hb], first, final)

                gate_up(0, static=True)
                gate_up(1)
                down(0, first=True)
                gate_up(2)
                down(1)
                with loop(pe, PAIRS - 1) as i:
                    gate_up(3, i)
                    down(2, i)
                    gate_up(4, i)
                    down(3, i)
                down(GROUPS - 1, final=True)

            pe.wait_ge(consts_built, 2)
            pe.wait_ge(consts_loaded, 48)
            nc.tensor.transpose(psum[:, 0, 0:64], gains_rows[:, :], ident[0:64, 0:64]).then_inc(gains_T, 1)
            for d in range(DC):
                if d % (DC // 2) == 0:
                    pe.wait_ge(x_loaded[d // (DC // 2)], 16)
                for t in range(TT):
                    last = nc.tensor.transpose(y_acc(d)[:, t * P:(t + 1) * P], x_tok[:, t, d * P:(d + 1) * P],
                                               ident[:, :])
                if d % 2 and d < DC - 1:
                    last.then_inc(y_done, 1)
            last.then_inc(xT_last, 1)
            pe.wait_ge(consts_built, 3)
            pe.wait_ge(gains_done, 1)

            ffn(FFN0, 0, 0)

            def qkv_tile(j, s, norm=None, stats_norm=None):
                n = ATT0 + 3 * j + s
                weights(n)
                if j:
                    pe.wait_ge(qkv_scaled, 3 * (j - 1) + s + 1)
                elif s == 0:
                    pe.wait_ge(up_scaled, GROUPS)
                if s < 2:
                    column_product(n, s, norm, stats_norm)
                    return
                hi, lo = col_tile(w_hi, n), col_tile(w_lo, n)
                for t in range(TT):
                    toks = slice(t * P, (t + 1) * P)
                    for k in range(DC):
                        out = psum[:, 2, t * GW:(t + 1) * GW]
                        nc.tensor.matmul(out, xg_hi[:, k, toks], hi[:, k, :], start=(k == 0), stop=False,
                                         skip_group_check=True)
                        nc.tensor.matmul(out, xg_hi[:, k, toks], lo[:, k, :], start=False, stop=False,
                                         skip_group_check=True)
                        last = nc.tensor.matmul(out, xg_lo[:, k, toks], hi[:, k, :], start=False, stop=(k == DC - 1),
                                                skip_group_check=True)
                last.then_inc(tile_used, 1)

            def out_tile(j, halfway=None):
                n = ATT0 + 3 * QUADS + j
                weights(n)
                pe.wait_ge(o_lo_done, max(j + 1, QUADS - 1))
                chunks = slice(GM * j, GM * (j + 1))
                row_product(n, o_hi[:, chunks, :], o_lo[:, chunks, :], first=(j == 0), final=(j == QUADS - 1),
                            halfway=halfway)

            def head_rows(hh):
                return slice(HD * (hh % 2), HD * (hh % 2) + HD)

            def scores(j, half):
                heads = (2 * half, 2 * half + 1)
                if half == 0:
                    pe.wait_ge(qkv_scaled, 3 * j + 2)
                for hh in heads:
                    H = QH * j + hh
                    if H >= QH:
                        pe.wait_ge(probT_copied, H - QH + 1)
                    if j == QUADS - 1 and hh == 3:
                        pe.wait_ge(probT_copied, H - 3 + 1)
                for q, keys, cols in ((slice(0, P), slice(0, P), slice(0, P)),
                                      (slice(P, SEQ), slice(0, SEQ), slice(P, SC))):
                    for hh in heads:
                        last = nc.tensor.matmul(bank(head_bank(j, hh))[:, cols], q_sb[head_rows(hh), j % 2, half, q],
                                                k_sb[head_rows(hh), j % 2, half, keys], start=True, stop=True,
                                                skip_group_check=True)
                last.then_inc(score_done, 2)

            def transposes(j, half):
                for hh in (2 * half, 2 * half + 1):
                    H = QH * j + hh
                    pe.wait_ge(prob_done, H + 1)
                    s = bank(head_bank(j, hh))
                    for b in range(3):
                        last = nc.tensor.transpose(s[:, b * P:(b + 1) * P], prob[:, H % 2, b * P:(b + 1) * P],
                                                   ident[:, :])
                    last.then_inc(probT_done, 1)

            def values(j, half):
                heads = (2 * half, 2 * half + 1)
                pe.wait_ge(probT_copied, QH * j + heads[1] + 1)
                if half == 0:
                    pe.wait_ge(qkv_scaled, 3 * (j + 1))
                    if j:
                        pe.wait_ge(o_lo_done, j)
                for t, toks, cols in ((0, slice(0, SEQ), slice(0, SEQ)), (1, slice(P, SEQ), slice(SEQ, SC))):
                    for hh in heads:
                        last = nc.tensor.matmul(acc_bank(o_bank(j))[head_rows(hh), half, toks],
                                                v_sb[:, j % 2, t, hh * HD:(hh + 1) * HD],
                                                probT[:, hh % 2, cols], start=(t == 0), stop=(t == 1),
                                                skip_group_check=True)
                last.then_inc(pv_done, 2)

            qkv_tile(0, 0, norm=1)
            qkv_tile(0, 1, stats_norm=1)
            qkv_tile(0, 2)
            for j in range(QUADS):
                def between(s):
                    if j < QUADS - 1:
                        qkv_tile(j + 1, s)
                    else:
                        out_tile(s)
                scores(j, 0)
                between(0)
                transposes(j, 0)
                scores(j, 1)
                between(1)
                values(j, 0)
                transposes(j, 1)
                if j < QUADS - 1:
                    between(2)
                    values(j, 1)
                else:
                    out_tile(2, halfway=lambda: values(j, 1))
            out_tile(QUADS - 1)

            ffn(FFN1, 1, 2)
            ffn(FFN2, 2, 3)

            weights(POOL0)
            pe.wait_ge(up_scaled, 3 * GROUPS)
            whi = w_hi[:, POOL0 % SPL, :].rearrange("p (g m e) -> p g m e", g=NPG, m=GM)
            wlo = w_lo[:, POOL0 % SPL, :].rearrange("p (g m e) -> p g m e", g=NPG, m=GM)
            for g in range(NPG):
                pe.wait_ge(xg_lo_done, 4 * DC + GM * (g + 1))
                for t in range(TT):
                    toks = slice(t * P, (t + 1) * P)
                    for m in range(GM):
                        k = GM * g + m
                        out = psum[:, g, t * GW:(t + 1) * GW]
                        nc.tensor.matmul(out, xg_hi[:, k, toks], whi[:, g, m, :], start=(m == 0), stop=False,
                                         skip_group_check=True)
                        nc.tensor.matmul(out, xg_hi[:, k, toks], wlo[:, g, m, :], start=False, stop=False,
                                         skip_group_check=True)
                        last = nc.tensor.matmul(out, xg_lo[:, k, toks], whi[:, g, m, :], start=False,
                                                stop=(m == GM - 1), skip_group_check=True)
            last.then_inc(tile_used, 1)
            statistics(4)
            pe.wait_ge(consts_built, CONSTS)
            for d in range(DC):
                g, m = d // GM, d % GM
                if m == 0:
                    pe.wait_ge(pool_u_scaled, g + 1)
                reach = P + WINDOWS[g] - 1
                nc.tensor.matmul(y_acc(d)[:, 0:reach], pool_u[:, g, 0, m * P:(m + 1) * P], band[:, g, 0, 0:reach],
                                 start=(d % 2 == 0), stop=False, skip_group_check=True)
                last = nc.tensor.matmul(y_acc(d)[:, P:SEQ], pool_u[:, g, 1, m * P:(m + 1) * P], band[:, g, 1, P:SEQ],
                                        start=False, stop=True, skip_group_check=True)
                if d % 2 and d < DC - 1:
                    last.then_inc(y_done, 1)
            last.then_inc(pooled, 1)

            ffn(FFN3, 3, 5)

            pe.wait_ge(up_scaled, 4 * GROUPS)
            for d in range(DC):
                pe.wait_ge(xn_done, d + 1)
                for t in range(TT):
                    last = nc.tensor.transpose(psum[:, 2 * t + d // 4, (d % 4) * P:(d % 4 + 1) * P],
                                               xn[:, d, t * P:(t + 1) * P], ident[:, :])
            last.then_inc(out_T, 1)
            statistics(6)

        def early_tiles(j, half):
            if j == 0:
                return (ATT0 + 6, ATT0 + 7) if half else (ATT0 + 5,)
            return (ATT0 + 6 + 3 * j + half,)

        def wait_pair(eng, norm, c):
            if c < DB - 1:
                eng.wait_ge(y_done, norm * (DB - 1) + c + 1)
            elif norm == 0:
                eng.wait_ge(xT_last, 1)
            elif norm == 5:
                eng.wait_ge(pooled, 1)
            else:
                eng.wait_ge(tile_used, used({1: ATT0, 2: FFN1, 3: FFN2, 4: POOL0, 6: TILES}[norm] - 1))


        @block.scalar
        def _(act):
            def split_hi(n, i=0):
                if n >= TILES:
                    return
                act.wait_ge(raw_loaded[n % RAW], 16 * (n // RAW + 1) + 16 * (BODY // RAW) * i)
                act.wait_ge(tile_used, n + 1 + BODY * i)
                nc.scalar.activation(w_hi[:, n % SPL, :], raw[:, n % RAW, :], ACT.Copy).then_inc(hi_split, 1)

            def round_x(norm):
                for c in range(DB):
                    act.wait_ge(x_done, norm * DB + c + 1)
                    for d in (2 * c, 2 * c + 1):
                        nc.scalar.activation(xg_hi[:, d, :], x[:, d, :], ACT.Copy,
                                             scale=gain(norm, d)).then_inc(xg_hi_done, 1)
                    if norm == 0:
                        act.wait_ge(piece_loaded[c] if c < DB - 1 else raw_loaded[0], 16)
                        piece = slice(2 * c * GW, (2 * c + 2) * GW)
                        nc.scalar.activation(w_hi[:, 0, piece], raw[:, 0, piece],
                                             ACT.Copy).then_inc(piece_hi if c < DB - 1 else hi_split, 1)
                    else:
                        square_x(c)

            def square_x(c):
                pair = slice(2 * c, 2 * c + 2)
                nc.scalar.activation(sq[:, pair, :], x[:, pair, :], ACT.Square).then_inc(sq_done, 1)

            def boundary(norm, n0):
                if norm:
                    if norm != 5:
                        split_hi(n0 + 1)
                    round_x(norm)
                else:
                    round_x(norm)
                    split_hi(n0 + 1)
                    for c in range(DB):
                        square_x(c)
                split_hi(n0 + 2)
                split_hi(n0 + 3)
                root(norm)

            def root(norm, r=rstd):
                act.wait_ge(inv_mean_done, norm + 1)
                nc.scalar.activation(r[:, :], r[:, :], ACT.Sqrt).then_inc(root_done, 1)

            def ffn(n0, index):
                g0 = index * GROUPS

                def step(j, i=0):
                    n = n0 + 3 * j + 3
                    if 0 < j < GROUPS - 1:
                        split_hi(n, i)
                    act.wait_ge(gate_scaled, g0 + j + 1 + 2 * i)
                    nc.scalar.activation(s_sb, g_sb, ACT.Silu).then_inc(silu_done, 1)
                    if j < GROUPS - 1:
                        split_hi(n + 1, i)
                    act.wait_ge(h_done, g0 + j + 1 + 2 * i)
                    nc.scalar.activation(h_hi[:, (g0 + j) % 2], h_sb, ACT.Copy).then_inc(h_hi_done, 1)
                    split_hi(n + 2 if j < GROUPS - 1 else n, i)
                    if j == GROUPS - 1 and n == POOL0:
                        split_hi(FFN3)

                step(0)
                with loop(act, PAIRS - 1) as i:
                    step(1, i)
                    step(2, i)
                step(GROUPS - 2)
                step(GROUPS - 1)

            norms = ln_gains.rearrange("l s (c p) -> (l s c) p", p=P)
            nrows = norms.shape[0]
            act.dma_start(gains_rows[0:nrows, :], norms).then_inc(consts_loaded, 16)
            act.dma_start(gains_rows[nrows:nrows + DC, :],
                          pool_scale[0].rearrange("(c p) -> c p", p=P)).then_inc(consts_loaded, 16)
            act.dma_start(gains_rows[nrows + DC:nrows + 2 * DC, :],
                          final_gain.rearrange("(c p) -> c p", p=P)).then_inc(consts_loaded, 16)
            nc.scalar.memzero(row_sum[:, 0, 0:1]).then_inc(warm, 1)
            act.wait_ge(warm, 1)
            nc.scalar.activation(row_sum[:, 0, 1:2], row_sum[:, 0, 0:1], ACT.Square)
            act.wait_ge(gains_done, 1)
            boundary(0, FFN0)
            ffn(FFN0, 0)
            boundary(1, ATT0)

            def exps(H):
                b = H % 2
                act.wait_ge(max_done, H + 1)
                nc.scalar.activation(prob[:, b, 0:P], score[:, b, 0:P], ACT.Exp, bias=neg_max[:, b, 0:1],
                                     accum_out=row_sum[:, b, 0:1])
                nc.scalar.activation(prob[:, b, P:SC], score[:, b, P:SC], ACT.Exp, bias=neg_max[:, b, 1:2],
                                     accum_out=row_sum[:, b, 1:2]).then_inc(exp_done, 1)

            def copy_probT(j, hh):
                H = QH * j + hh
                act.wait_ge(probT_done, H + 1)
                nc.scalar.activation(probT[:, H % 2, :], bank(head_bank(j, hh))[:, 0:SC],
                                     ACT.Copy).then_inc(probT_copied, 1)

            split_hi(ATT0 + 4)
            for j in range(QUADS):
                for half in range(2):
                    heads = (2 * half, 2 * half + 1)
                    for hh in heads:
                        exps(QH * j + hh)
                    if j < QUADS - 1:
                        for n in early_tiles(j, half):
                            split_hi(n)
                    for hh in heads:
                        copy_probT(j, hh)
                    if j == QUADS - 1:
                        split_hi(ATT0 + 6 + 3 * j + half)
                if j < QUADS - 1:
                    split_hi(ATT0 + 8 + 3 * j)
                act.wait_ge(pv_done, QH * (j + 1))
                nc.scalar.activation(o_hi[:, GM * j:GM * (j + 1), :], acc_bank(o_bank(j)),
                                     ACT.Copy).then_inc(o_hi_done, 1)
            boundary(2, FFN1)
            ffn(FFN1, 1)
            boundary(3, FFN2)
            ffn(FFN2, 2)

            round_x(4)
            split_hi(FFN3 + 1)
            root(4, rstd_p)
            act.wait_ge(rstd_done, 5)
            act.wait_ge(tile_used, used(POOL0))
            for g in range(NPG):
                for t in range(TT):
                    last = nc.scalar.activation(pool_u[:, g, t, :], psum[:, g, t * GW:(t + 1) * GW], ACT.Copy,
                                                scale=rstd_p[:, t:t + 1])
                last.then_inc(pool_u_scaled, 1)
            boundary(5, FFN3)
            ffn(FFN3, 3)

            for d in range(DC):
                act.wait_ge(x_done, 6 * DB + d // 2 + 1)
                if d % 2 == 0:
                    square_x(d // 2)
                nc.scalar.activation(xn[:, d, :], x[:, d, :], ACT.Copy, scale=gain(6, d)).then_inc(xn_done, 1)
            root(6, rstd_p)
            act.wait_ge(out_T, 1)
            act.wait_ge(rstd_done, 7)
            for t in range(TT):
                nc.scalar.activation(x_tok[:, t, 0:512], bank(2 * t), ACT.Copy,
                                     scale=rstd_p[:, t:t + 1]).then_inc(out_scaled_act, 1)

        @block.vector
        def _(dve):
            dve.sem_inc(lo_split, RAW)

            def split_lo(n, i=0):
                if n >= TILES:
                    return
                dve.wait_ge(hi_split, n + 1 + BODY * i)
                nc.vector.tensor_tensor(w_lo[:, n % SPL, :], raw[:, n % RAW, :], w_hi[:, n % SPL, :].bitcast(f32),
                                        ALU.subtract).then_inc(lo_split, 1)

            def update_x(norm, scalar=None, split=True, per_chunk=False, squares=False):
                for c in range(DB + 1):
                    if c < DB:
                        wait_pair(dve, norm, c)
                        pair = acc_bank(4 + c)
                        xs = x[:, 2 * c:2 * c + 2, :]
                        if norm == 0:
                            ins = nc.vector.tensor_copy(xs, pair)
                        elif per_chunk:
                            for e in range(2):
                                ins = nc.vector.scalar_tensor_tensor(out=xs[:, e, :], in0=pair[:, e, :],
                                                                     scalar=scalar(2 * c + e), in1=xs[:, e, :],
                                                                     op0=ALU.mult, op1=ALU.add)
                        else:
                            ins = nc.vector.scalar_tensor_tensor(out=xs, in0=pair, scalar=scalar, in1=xs,
                                                                 op0=ALU.mult, op1=ALU.add)
                        ins.then_inc(x_done, 1)
                    if c and split:
                        for d in (2 * c - 2, 2 * c - 1):
                            dve.wait_ge(xg_hi_done, norm * DC + d + 1)
                            nc.vector.scalar_tensor_tensor(out=xg_lo[:, d, :], in0=x[:, d, :], scalar=gain(norm, d),
                                                           in1=xg_hi[:, d, :].bitcast(f32),
                                                           op0=ALU.mult, op1=ALU.subtract).then_inc(xg_lo_done, 1)
                    if c and norm == 0:
                        piece = slice((2 * c - 2) * GW, 2 * c * GW)
                        if c < DB:
                            dve.wait_ge(piece_hi, c)
                        else:
                            dve.wait_ge(hi_split, 1)
                        nc.vector.tensor_tensor(w_lo[:, 0, piece], raw[:, 0, piece], w_hi[:, 0, piece].bitcast(f32),
                                                ALU.subtract).then_inc(piece_lo if c < DB else lo_split, 1)
                    if squares and c > 1:
                        add_squares(norm, c - 1)

            def add_squares(norm, c):
                dve.wait_ge(sq_done, norm * DB + c + 1)
                if c > 1:
                    dve.wait_ge(sq_added, norm * (DB - 1) + c - 1)
                nc.vector.tensor_tensor(sq[:, 0:2, :], sq[:, 0:2, :], sq[:, 2 * c:2 * c + 2, :],
                                        ALU.add).then_inc(sq_added, 1)

            def fold_squares(norm):
                dve.wait_ge(sq_added, (norm + 1) * (DB - 1))
                nc.vector.tensor_tensor(sq_sum[:, :], sq[:, 0, :], sq[:, 1, :], ALU.add).then_inc(sq_sum_done, 1)

            def sum_squares(norm):
                for c in range(1, DB):
                    add_squares(norm, c)
                fold_squares(norm)

            def newton_step(ins):
                steps[0] += 1
                ins.then_inc(newton, 1)
                dve.wait_ge(newton, steps[0])

            steps = [0]

            def inverse_mean(norm, cols=slice(0, SEQ + TT)):
                dve.wait_ge(stats_done, norm + 1)
                newton_step(nc.vector.tensor_scalar(mean[:, cols], psum[:, 4, cols], 1.0 / D, EPS,
                                                    ALU.mult, ALU.add))
                nc.vector.reciprocal(rstd[:, cols], mean[:, cols]).then_inc(inv_mean_done, 1)

            def refine_rstd(norm, cols=slice(0, SEQ + TT)):
                r, m, rr = rstd[:, cols], mean[:, cols], rms_sq[:, cols]
                dve.wait_ge(root_done, norm + 1)
                newton_step(nc.vector.tensor_tensor(rr, r, r, ALU.mult))
                newton_step(nc.vector.scalar_tensor_tensor(out=rr, in0=rr, scalar=-0.5, in1=m,
                                                           op0=ALU.mult, op1=ALU.mult))
                nc.vector.scalar_tensor_tensor(out=r, in0=rr, scalar=1.5, in1=r,
                                               op0=ALU.add, op1=ALU.mult).then_inc(rstd_done, 1)

            def boundary(norm, n0, scalar=None, per_chunk=False):
                update_x(norm, scalar, per_chunk=per_chunk)
                if norm != 5:
                    split_lo(n0 + 1)
                sum_squares(norm)
                split_lo(n0 + 2)
                inverse_mean(norm)
                split_lo(n0 + 3)
                refine_rstd(norm)
                dve.wait_ge(rstd_done, norm + 1)

            rstd_m = rstd_t.unsqueeze(1).broadcast_to([P, GM, SEQ])

            def ffn(n0, index):
                g0 = index * GROUPS

                def step(j, i=0):
                    n = n0 + 3 * j + 3
                    gate_n, up_n = n0 + gate_tile(j), n0 + up_tile(j)
                    dve.wait_ge(tile_used, used(gate_n, i))
                    nc.vector.tensor_tensor(g_sb, acc_bank(2 * ((g0 + j) % 2)), rstd_m,
                                            ALU.mult).then_inc(gate_scaled, 1)
                    if 0 < j < GROUPS - 1:
                        split_lo(n, i)
                    dve.wait_ge(tile_used, used(up_n, i))
                    nc.vector.tensor_tensor(u_sb, acc_bank(2 * ((g0 + j) % 2) + 1), rstd_m,
                                            ALU.mult).then_inc(up_scaled, 1)
                    dve.wait_ge(silu_done, g0 + j + 1 + 2 * i)
                    dve.wait_ge(up_scaled, g0 + j + 1 + 2 * i)
                    nc.vector.tensor_tensor(h_sb, s_sb, u_sb, ALU.mult).then_inc(h_done, 1)
                    if j < GROUPS - 1:
                        split_lo(n + 1, i)
                    dve.wait_ge(h_hi_done, g0 + j + 1 + 2 * i)
                    nc.vector.tensor_tensor(h_lo[:, (g0 + j) % 2], h_sb, h_hi[:, (g0 + j) % 2].bitcast(f32),
                                            ALU.subtract).then_inc(h_lo_done, 1)
                    split_lo(n + 2 if j < GROUPS - 1 else n, i)
                    if j == GROUPS - 1 and n == POOL0:
                        split_lo(FFN3)

                step(0)
                with loop(dve, PAIRS - 1) as i:
                    step(1, i)
                    step(2, i)
                step(GROUPS - 2)
                step(GROUPS - 1)

            dve.wait_ge(gains_T, 1)
            nc.vector.tensor_copy(gains[:, :], psum[:, 0, 0:64]).then_inc(gains_done, 1)
            dve.wait_ge(gains_done, 1)
            boundary(0, FFN0)
            dve.wait_ge(consts_built, COUNTS)
            nc.vector.reciprocal(count[:, :, :], count[:, :, :]).then_inc(inv_cnt_done, 1)
            ffn(FFN0, 0)
            boundary(1, ATT0, 0.5)

            def qkv_scale(j, s):
                dve.wait_ge(tile_used, used(ATT0 + 3 * j + s))
                if s == 0:
                    ins = nc.vector.scalar_tensor_tensor(out=q_sb[:, j % 2], in0=acc_bank(0), scalar=HD ** -0.5,
                                                         in1=rstd_m, op0=ALU.mult, op1=ALU.mult)
                elif s == 1:
                    ins = nc.vector.tensor_tensor(k_sb[:, j % 2], acc_bank(1), rstd_m, ALU.mult)
                else:
                    for t in range(TT):
                        ins = nc.vector.tensor_scalar(v_sb[:, j % 2, t, :], psum[:, 2, t * GW:(t + 1) * GW],
                                                      rstd_p[:, t:t + 1], None, ALU.mult)
                ins.then_inc(qkv_scaled, 1)

            def bias_and_max(j, hh):
                H = QH * j + hh
                b = H % 2
                slope = 2.0 ** (-8.0 * (H + 1) / HEADS)
                dve.wait_ge(score_done, H + 1)
                nc.vector.scalar_tensor_tensor(out=score[:, b, :], in0=dist[:, :], scalar=-slope,
                                               in1=bank(head_bank(j, hh))[:, 0:SC], op0=ALU.mult,
                                               op1=ALU.add).then_inc(score_biased, 1)
                dve.wait_ge(score_biased, H + 1)
                nc.vector.tensor_reduce(neg_max[:, b, 0:1], score[:, b, 0:P], AX.X, ALU.max, negate=True)
                nc.vector.tensor_reduce(neg_max[:, b, 1:2], score[:, b, P:SC], AX.X, ALU.max,
                                        negate=True).then_inc(max_done, 1)

            def normalise(H):
                b = H % 2
                dve.wait_ge(exp_done, H + 1)
                nc.vector.reciprocal(row_inv[:, b, :], row_sum[:, b, :]).then_inc(inv_done, 1)
                dve.wait_ge(inv_done, H + 1)
                nc.vector.tensor_scalar(prob[:, b, 0:P], prob[:, b, 0:P], row_inv[:, b, 0:1], None, ALU.mult)
                nc.vector.tensor_scalar(prob[:, b, P:SC], prob[:, b, P:SC], row_inv[:, b, 1:2], None,
                                        ALU.mult).then_inc(prob_done, 1)

            dve.wait_ge(consts_built, CONSTS)
            qkv_scale(0, 0)
            qkv_scale(0, 1)
            split_lo(ATT0 + 4)
            for j in range(QUADS):
                for half in range(2):
                    heads = (2 * half, 2 * half + 1)
                    for hh in heads:
                        bias_and_max(j, hh)
                    for hh in heads:
                        normalise(QH * j + hh)
                    if j == 0 and half == 0:
                        qkv_scale(0, 2)
                    for n in early_tiles(j, half):
                        split_lo(n)
                    if j < QUADS - 1:
                        qkv_scale(j + 1, half)
                if j < QUADS - 1:
                    split_lo(ATT0 + 8 + 3 * j)
                    qkv_scale(j + 1, 2)
                dve.wait_ge(o_hi_done, j + 1)
                nc.vector.tensor_tensor(o_lo[:, GM * j:GM * (j + 1), :], acc_bank(o_bank(j)),
                                        o_hi[:, GM * j:GM * (j + 1), :].bitcast(f32),
                                        ALU.subtract).then_inc(o_lo_done, 1)
            boundary(2, FFN1, 1.0)
            ffn(FFN1, 1)
            boundary(3, FFN2, 0.5)
            ffn(FFN2, 2)
            update_x(4, 0.5, squares=True)
            fold_squares(4)
            inverse_mean(4, slice(SEQ, SEQ + TT))
            refine_rstd(4, slice(SEQ, SEQ + TT))
            split_lo(FFN3 + 1)
            boundary(5, FFN3, lambda d: gains[:, POOL_SCALE_COL + d:POOL_SCALE_COL + d + 1], per_chunk=True)
            ffn(FFN3, 3)
            update_x(6, 0.5, split=False, squares=True)
            fold_squares(6)
            inverse_mean(6, slice(SEQ, SEQ + TT))
            refine_rstd(6, slice(SEQ, SEQ + TT))
            dve.wait_ge(out_T, 1)
            dve.wait_ge(rstd_done, 7)
            for t in range(TT):
                nc.vector.tensor_scalar(x_tok[:, t, 512:1024], bank(2 * t + 1), rstd_p[:, t:t + 1], None,
                                        ALU.mult).then_inc(out_scaled_dve, 1)


_INS = ["x", "ln_gains", "ffn_w_gate", "ffn_w_up", "ffn_w_down", "attn_w_qkv", "attn_w_o", "pool_w", "pool_scale",
        "final_gain"]


def kernel(**inputs):
    import numpy as np
    import concourse.bacc as bacc
    from concourse.bass_utils import run_bass_kernel_spmd

    nc = bacc.Bacc("TRN2", target_bir_lowering=False, num_devices=1)
    arrays, args = {}, []
    for name in _INS:
        a = np.ascontiguousarray(inputs[name])
        arrays[f"in_{name}_dram"] = a
        args.append(nc.dram_tensor(f"in_{name}_dram", a.shape, mybir.dt.from_np(a.dtype), kind="ExternalInput").ap())
    shape = inputs["x"].shape
    out = nc.dram_tensor("out_dram", shape, mybir.dt.float32, kind="ExternalOutput").ap()
    build_trunk(nc, *args, out)
    r = run_bass_kernel_spmd(nc, [arrays], core_ids=[0])
    return r.results[0]["out_dram"]
```
